# Optimizing a Trainium2 kernel written in Bass

```python
import math
import jax
import jax.numpy as jnp
from jax import lax
import numpy as np

"""Four layers of a chunk-causal hybrid streaming-encoder trunk.

Even layers: one combined input projection feeds two parallel head groups:
  (A) DSA-style sparse attention (lightweight ReLU indexer, per-query top-k key gather, QK-norm, NoPE)
  (B) S5-style complex-diagonal SSM (16-channel groups, 64-dim complex state each, ZOH, associative scan, GELU + GLU)
  Outputs are concatenated and passed through one output projection.
Odd layers: short gated convolution mixer y = W_out(B * conv3(C * (W_in x))).
Every layer then cross-attends (4 heads) into the memory tokens and applies a gated MLP with a causal
depthwise width-3 convolution on the activation branch. Pre-RMSNorm before every sub-layer.

Inputs: x (BATCH, SEQ, D_MODEL), mem (BATCH, 256, D_MODEL) plus per-layer parameters.
Output: (BATCH, SEQ, D_MODEL).
"""

D_MODEL = 1024
BATCH = 1
SEQ = 1024
DEPTH = 2

CHUNK = 64
N_MEM = 256
EPS = 1e-6

A_HEADS = 8
A_HEAD_DIM = 64
A_WIDTH = A_HEADS * A_HEAD_DIM
IDX_HEADS = 4
IDX_DIM = 64
TOPK_MAX = 256
Q_BLOCK = 128

S5_WIDTH = D_MODEL - A_WIDTH
S5_GROUP = 16
S5_GROUPS = S5_WIDTH // S5_GROUP
S5_STATE = 64

CONV_WIDTH = 3

X_HEADS = 4
X_HEAD_DIM = 128
X_WIDTH = X_HEADS * X_HEAD_DIM

D_FF = 2816

N_EVEN = (DEPTH + 1) // 2
N_ODD = DEPTH // 2

EVEN_SPLIT_SIZES = (A_WIDTH, A_HEAD_DIM, A_HEAD_DIM, IDX_HEADS * IDX_DIM, IDX_DIM, IDX_HEADS, S5_WIDTH)
EVEN_IN = A_WIDTH + 2 * A_HEAD_DIM + IDX_HEADS * IDX_DIM + IDX_DIM + IDX_HEADS + S5_WIDTH

kernel_name = "hybrid_dsa_s5_shortconv_trunk"

def rms_norm(x, g):
    xf = x.astype(jnp.float32)
    xf = xf * lax.rsqrt(jnp.mean(xf * xf, axis=-1, keepdims=True) + EPS)
    return (xf * g.astype(jnp.float32)).astype(x.dtype)

def causal_dwconv(z, w, b):
    T = z.shape[1]
    zp = jnp.pad(z, ((0, 0), (CONV_WIDTH - 1, 0), (0, 0)))
    y = w[0] * zp[:, 0:T] + w[1] * zp[:, 1:T + 1] + w[2] * zp[:, 2:T + 2]
    return y + b

def dsa_attention(q, k, v, iq, ik, iw):
    B, T = q.shape[0], q.shape[1]
    topk = min(TOPK_MAX, T // 4)
    nb = T // Q_BLOCK
    key_pos = jnp.arange(T)
    idx_scale = (IDX_DIM ** -0.5) * (IDX_HEADS ** -0.5)
    att_scale = A_HEAD_DIM ** -0.5

    def to_blocks(a):
        return jnp.moveaxis(a.reshape((B, nb, Q_BLOCK) + a.shape[2:]), 1, 0)

    def block(args):
        blk, qb, iqb, iwb = args
        t = blk * Q_BLOCK + jnp.arange(Q_BLOCK)
        limit = (t // CHUNK + 1) * CHUNK
        adm = key_pos[None, :] < limit[:, None]
        rel = jax.nn.relu(jnp.einsum('bqhd,bsd->bqhs', iqb, ik))
        score = jnp.einsum('bqh,bqhs->bqs', iwb, rel) * idx_scale
        score = jnp.where(adm[None], score.astype(jnp.float32), -jnp.inf)
        _, sel = lax.top_k(score, topk)
        valid = sel < limit[None, :, None]
        kg = jax.vmap(lambda kk, ii: kk[ii])(k, sel)
        vg = jax.vmap(lambda vv, ii: vv[ii])(v, sel)
        s = jnp.einsum('bqhd,bqkd->bhqk', qb, kg).astype(jnp.float32) * att_scale
        s = jnp.where(valid[:, None], s, -jnp.inf)
        p = jax.nn.softmax(s, axis=-1).astype(v.dtype)
        return jnp.einsum('bhqk,bqkd->bqhd', p, vg)

    out = lax.map(block, (jnp.arange(nb), to_blocks(q), to_blocks(iq), to_blocks(iw)))
    return jnp.moveaxis(out, 0, 1).reshape(B, T, A_WIDTH)

def s5_mixer(u, lam_re, lam_im, log_step, b_re, b_im, c_re, c_im, d, w_glu, b_glu):
    B, T, _ = u.shape
    f32 = jnp.float32
    uf = u.astype(f32).reshape(B, T, S5_GROUPS, S5_GROUP)
    lam = lax.complex(lam_re.astype(f32), lam_im.astype(f32))
    delta = jnp.exp(log_step.astype(f32))[:, None]
    lam_bar = jnp.exp(lam * delta)
    b_bar = ((lam_bar - 1.0) / lam)[..., None] * lax.complex(b_re.astype(f32), b_im.astype(f32))
    bu = jnp.einsum('gpc,btgc->btgp', b_bar, uf.astype(jnp.complex64))
    a = jnp.broadcast_to(lam_bar, (1, T) + lam_bar.shape)

    def combine(e1, e2):
        a1, b1 = e1
        a2, b2 = e2
        return a1 * a2, a2 * b1 + b2

    _, h = lax.associative_scan(combine, (a, bu), axis=1)
    c = lax.complex(c_re.astype(f32), c_im.astype(f32))
    y = jnp.einsum('gcp,btgp->btgc', c, h).real + d.astype(f32).reshape(S5_GROUPS, S5_GROUP) * uf
    y = jax.nn.gelu(y.reshape(B, T, S5_WIDTH)).astype(u.dtype)
    return y * jax.nn.sigmoid(y @ w_glu + b_glu)

def even_mixer(h, w_in, w_out, q_norm, k_norm, lam_re, lam_im, log_step, b_re, b_im, c_re, c_im, d, w_glu, b_glu):
    B, T, _ = h.shape
    split_pts = np.cumsum(EVEN_SPLIT_SIZES)[:-1].tolist()
    q, k, v, iq, ik, iw, u = jnp.split(h @ w_in, split_pts, axis=-1)
    q = rms_norm(q.reshape(B, T, A_HEADS, A_HEAD_DIM), q_norm)
    k = rms_norm(k, k_norm)
    ya = dsa_attention(q, k, v, iq.reshape(B, T, IDX_HEADS, IDX_DIM), ik, iw)
    yb = s5_mixer(u, lam_re, lam_im, log_step, b_re, b_im, c_re, c_im, d, w_glu, b_glu)
    return jnp.concatenate([ya, yb], axis=-1) @ w_out

def short_conv_mixer(h, w_in, conv_w, conv_b, w_out):
    gb, gc, z = jnp.split(h @ w_in, 3, axis=-1)
    return (gb * causal_dwconv(gc * z, conv_w, conv_b)) @ w_out

def memory_cross_attention(h, m, w_q, w_kv, w_o, q_norm, k_norm):
    B, T, _ = h.shape
    M = m.shape[1]
    q = rms_norm((h @ w_q).reshape(B, T, X_HEADS, X_HEAD_DIM), q_norm)
    k, v = jnp.split(m @ w_kv, 2, axis=-1)
    k = rms_norm(k.reshape(B, M, X_HEADS, X_HEAD_DIM), k_norm)
    v = v.reshape(B, M, X_HEADS, X_HEAD_DIM)
    s = jnp.einsum('bthd,bmhd->bhtm', q, k).astype(jnp.float32) * (X_HEAD_DIM ** -0.5)
    p = jax.nn.softmax(s, axis=-1).astype(v.dtype)
    o = jnp.einsum('bhtm,bmhd->bthd', p, v).reshape(B, T, X_WIDTH)
    return o @ w_o

def conv_glu_ffn(h, w_up, conv_w, conv_b, w_down):
    g, u = jnp.split(h @ w_up, 2, axis=-1)
    return (jax.nn.silu(causal_dwconv(g, conv_w, conv_b)) * u) @ w_down

def setup_inputs(seed: int = 0) -> dict:
    key = jax.random.key(seed)
    ks = iter(jax.random.split(key, 48))
    f32 = jnp.float32

    def nrm(shape, fan_in):
        return jax.random.normal(next(ks), shape, f32) * (fan_in ** -0.5)

    def gain(shape):
        return 1.0 + 0.05 * jax.random.normal(next(ks), shape, f32)

    def small(shape):
        return 0.01 * jax.random.normal(next(ks), shape, f32)

    D = D_MODEL
    lam_im_base = math.pi * jnp.arange(S5_STATE, dtype=f32)
    return {
        "x": jax.random.normal(next(ks), (BATCH, SEQ, D), f32),
        "mem": jax.random.normal(next(ks), (BATCH, N_MEM, D), f32),
        "norm_mix": gain((DEPTH, D)),
        "norm_x": gain((DEPTH, D)),
        "norm_mem": gain((DEPTH, D)),
        "norm_ffn": gain((DEPTH, D)),
        "even_w_in": nrm((N_EVEN, D, EVEN_IN), D),
        "even_w_out": nrm((N_EVEN, D, D), D),
        "a_q_norm": gain((N_EVEN, A_HEAD_DIM)),
        "a_k_norm": gain((N_EVEN, A_HEAD_DIM)),
        "s5_lam_re": -0.5 + small((N_EVEN, S5_GROUPS, S5_STATE)),
        "s5_lam_im": lam_im_base + small((N_EVEN, S5_GROUPS, S5_STATE)),
        "s5_log_step": jax.random.uniform(next(ks), (N_EVEN, S5_GROUPS), f32, math.log(1e-3), math.log(1e-1)),
        "s5_b_re": nrm((N_EVEN, S5_GROUPS, S5_STATE, S5_GROUP), 2 * S5_GROUP),
        "s5_b_im": nrm((N_EVEN, S5_GROUPS, S5_STATE, S5_GROUP), 2 * S5_GROUP),
        "s5_c_re": nrm((N_EVEN, S5_GROUPS, S5_GROUP, S5_STATE), S5_STATE),
        "s5_c_im": nrm((N_EVEN, S5_GROUPS, S5_GROUP, S5_STATE), S5_STATE),
        "s5_d": jax.random.normal(next(ks), (N_EVEN, S5_WIDTH), f32),
        "s5_w_glu": nrm((N_EVEN, S5_WIDTH, S5_WIDTH), S5_WIDTH),
        "s5_b_glu": small((N_EVEN, S5_WIDTH)),
        "odd_w_in": nrm((N_ODD, D, 3 * D), D),
        "odd_conv_w": nrm((N_ODD, CONV_WIDTH, D), CONV_WIDTH),
        "odd_conv_b": small((N_ODD, D)),
        "odd_w_out": nrm((N_ODD, D, D), D),
        "x_w_q": nrm((DEPTH, D, X_WIDTH), D),
        "x_w_kv": nrm((DEPTH, D, 2 * X_WIDTH), D),
        "x_w_o": nrm((DEPTH, X_WIDTH, D), X_WIDTH),
        "x_q_norm": gain((DEPTH, X_HEAD_DIM)),
        "x_k_norm": gain((DEPTH, X_HEAD_DIM)),
        "f_w_up": nrm((DEPTH, D, 2 * D_FF), D),
        "f_conv_w": nrm((DEPTH, CONV_WIDTH, D_FF), CONV_WIDTH),
        "f_conv_b": small((DEPTH, D_FF)),
        "f_w_down": nrm((DEPTH, D_FF, D), D_FF),
    }

def reference(x, mem, norm_mix, norm_x, norm_mem, norm_ffn, even_w_in, even_w_out, a_q_norm, a_k_norm,
              s5_lam_re, s5_lam_im, s5_log_step, s5_b_re, s5_b_im, s5_c_re, s5_c_im, s5_d, s5_w_glu, s5_b_glu,
              odd_w_in, odd_conv_w, odd_conv_b, odd_w_out, x_w_q, x_w_kv, x_w_o, x_q_norm, x_k_norm,
              f_w_up, f_conv_w, f_conv_b, f_w_down):
    for i in range(DEPTH):
        j = i // 2
        h = rms_norm(x, norm_mix[i])
        if i % 2 == 0:
            x = x + even_mixer(h, even_w_in[j], even_w_out[j], a_q_norm[j], a_k_norm[j],
                               s5_lam_re[j], s5_lam_im[j], s5_log_step[j], s5_b_re[j], s5_b_im[j],
                               s5_c_re[j], s5_c_im[j], s5_d[j], s5_w_glu[j], s5_b_glu[j])
        else:
            x = x + short_conv_mixer(h, odd_w_in[j], odd_conv_w[j], odd_conv_b[j], odd_w_out[j])
        x = x + memory_cross_attention(rms_norm(x, norm_x[i]), rms_norm(mem, norm_mem[i]),
                                       x_w_q[i], x_w_kv[i], x_w_o[i], x_q_norm[i], x_k_norm[i])
        x = x + conv_glu_ffn(rms_norm(x, norm_ffn[i]), f_w_up[i], f_conv_w[i], f_conv_b[i], f_w_down[i])
    return x


_drawn_inputs = setup_inputs


def setup_inputs(seed=0):
    import zlib

    import numpy as np

    out = dict(_drawn_inputs(seed))
    spreads = {}
    factors = {'norm_x': 6.751,
     'norm_mem': 4.412,
     'a_q_norm': 8.0,
     'a_k_norm': 8.0,
     's5_lam_re': 8.0,
     's5_b_glu': 8.0,
     'odd_conv_b': 8.0,
     'x_q_norm': 6.308,
     'x_k_norm': 6.539,
     'f_conv_b': 7.188}
    for name, (base, spread) in spreads.items():
        noise = np.random.default_rng([zlib.crc32(name.encode()), seed]).standard_normal(out[name].shape)
        drawn = base * np.exp(spread * noise) if base else spread * noise
        out[name] = jnp.asarray(drawn.astype(out[name].dtype))
    for name, factor in factors.items():
        out[name] = (out[name] * factor).astype(out[name].dtype)
    return out
```

```python
from contextlib import ExitStack

import concourse.bass as bass
from concourse import mybir

F32 = mybir.dt.float32
R32 = mybir.dt.float32r
ACT = mybir.ActivationFunctionType
ALU = mybir.AluOpType
AXX = mybir.AxisListType.X

P = 128
D = 1024
T = 1024
KT = D // P
HALF = 512
NBLK = T // P
CHUNK = 64
TOPK = 256
AH, AD = 8, 64
IH = 4
S5L = 8
NCH = T // S5L
NG, GC, NS = 32, 16, 64
NPR = NG // 2
M = 256
XH = 4
FF = 2816
FT = FF // P
GRP = 2
NGRP = FT // GRP
OGRP = KT // GRP
EPS = 1e-6
NEG = -1.0e30
VW = AD + IH
TWO_PI = 6.283185307179586
PI_A = 6.28125
PI_B = 0.0019350051879882812
PI_C = TWO_PI - PI_A - PI_B

RAW, WSL = 2, 4

PHASES = [("in", 12, 12), ("glu", 2, 4), ("out", 8, 8)]
for _l in range(2):
    if _l == 1:
        PHASES += [("odd", OGRP * 8, OGRP * 14)]
    PHASES += [(f"xk{_l}", 4, 4), (f"xv{_l}", 4, 1), (f"xq{_l}", 4, 4), (f"xo{_l}", 4, 8),
               (f"mlp{_l}", NGRP * 6, NGRP * 12)]
PANEL0, TILE0 = {}, {}
_p = _t = 0
for _n, _a, _b in PHASES:
    PANEL0[_n], TILE0[_n] = _p, _t
    _p += _a
    _t += _b
NPANEL, NTILE = _p, _t

PCOLS = {}
_c = 0
for _n, _w in ([("mix0", 8), ("mix1", 8), ("x0", 8), ("x1", 8), ("mem0", 8), ("mem1", 8), ("ffn0", 8), ("ffn1", 8),
                ("aq", 1), ("ak", 1), ("xq0", 1), ("xq1", 1), ("xk0", 1), ("xk1", 1), ("bglu", 4),
                ("ocw", 24), ("ocb", 8)]
               + [(f"fcw{l}", 3 * FT) for l in range(2)] + [(f"fcb{l}", FT) for l in range(2)]
               + [("lre", NPR), ("lim", NPR), ("lstep", NPR), ("bre", NPR * GC), ("bim", NPR * GC),
                  ("cre", NPR * GC), ("cim", NPR * GC), ("d", NG)]):
    PCOLS[_n] = _c
    _c += _w
NSMALL = PCOLS["lre"]
NPAR = _c


GROUPED_NORM = {"mlp0": "ffn0", "odd": "mix1", "mlp1": "ffn1"}
NORMS = ["mix0", "x0", "ffn0", "mix1", "x1", "ffn1", "end"]


def norm_base(name, tag):
    before = NORMS[:NORMS.index(tag)]
    if name in ("nb", "diag", "R"):
        return sum(t not in ("x0", "x1") for t in before)
    if name == "x":
        return KT * sum(t != "mix0" for t in before)
    return len(before) * {"gh": KT, "sqt": KT, "gx": KT, "sqa": KT - 1}.get(name, 1)


def grouped_base(name, tag):
    if name == "used":
        return 1 + {"mlp0": 0, "odd": NGRP, "mlp1": NGRP + OGRP}[tag]
    if name == "act":
        return {"mlp0": 0, "mlp1": FT}[tag]
    return {"mlp0": 0, "odd": FT, "mlp1": FT + KT}[tag]


def build(nc, A):
    ctx = ExitStack()
    with ctx:
        sems = {}

        def S(name):
            if name not in sems:
                sems[name] = ctx.enter_context(nc.semaphore(name))
            return sems[name]

        base = [16512]

        def region(nbytes):
            at = base[0]
            base[0] += (nbytes + 31) // 32 * 32
            return at

        def at(name, shape, dt, offset):
            return nc.alloc_sbuf_tensor_at(name, shape, dt, offset=offset)

        K = 1024
        oX, oGX, oRAW, oWS, oHID = region(32 * K), region(64 * K), region(RAW * 4 * K), region(WSL * 8 * K), region(32 * K)
        oKV, oR, oSQ = region(8 * K), region(4 * K), region(4 * K)
        oT0 = region(4 * (T + 8))
        oT = [oT0] + [region(4 * K) for _ in range(4)]
        oPAR = region(4 * NSMALL)
        oCON = region(4 * (P * 3 + 8))
        oSM = region(4 * (8 + 8 + 64 + 64 + 8 + 8))
        assert base[0] <= 229344, base[0]

        X = at("X", [P, KT, T], F32, oX)
        GH = at("GH", [P, KT, T], R32, oGX)
        GL = at("GL", [P, KT, T], R32, oGX + 32 * K)
        RAWS = at("RAWS", [P, RAW, 8, P], F32, oRAW)
        WH = at("WH", [P, WSL, 8, P], R32, oWS)
        WL = at("WL", [P, WSL, 8, P], R32, oWS + WSL * 4 * K)
        HH = at("HH", [P, 2 * GRP, T], R32, oHID)
        HL = at("HL", [P, 2 * GRP, T], R32, oHID + 16 * K)
        R = at("R", [P, T], F32, oR)
        SQ = at("SQ", [P, T], F32, oSQ)
        T0 = at("T0", [P, T + 8], F32, oT[0])
        TT = [None] + [at(f"T{i}", [P, T], F32, oT[i]) for i in range(1, 5)]
        PAR = at("PAR", [P, NSMALL], F32, oPAR)
        ident = at("ident", [P, P], F32, oCON)
        ones = at("ones", [P, P], F32, oCON + 4 * P)
        bones = at("bones", [P, P], F32, oCON + 8 * P)
        epsc = at("epsc", [P, 8], F32, oCON + 12 * P)
        rT = at("rT", [P, NBLK], F32, oSM)
        rTa = at("rTa", [P, NBLK], F32, oSM + 32)
        fq = at("fq", [P, 64], F32, oSM + 64)
        fqa = at("fqa", [P, 64], F32, oSM + 64 + 256)
        sm1 = at("sm1", [P, 8], F32, oSM + 64 + 512)
        sm2 = at("sm2", [P, 8], F32, oSM + 64 + 544)

        Q = at("Q", [P, 4, T], F32, oHID)
        KK = at("KK", [P, T], F32, oHID + 16 * K)
        IQ = at("IQ", [P, 2, T], F32, oHID + 20 * K)
        IK = at("IK", [P, T], F32, oHID + 28 * K)
        WVR = at("WVR", [P, 8, VW], F32, oKV)
        WVH = at("WVH", [P, 8, VW], R32, oKV + 2176)
        WVL = at("WVL", [P, 8, VW], R32, oKV + 2 * 2176)
        VV = at("VV", [P, NBLK, VW], F32, oR + 4608)
        SC = at("SC", [P, T], F32, oX)
        WK = at("WK", [P, T], F32, oX + 4 * K)
        BI = at("BI", [P, T], F32, oX + 8 * K)
        EQ = at("EQ", [P, T], F32, oX + 12 * K)
        PF = at("PF", [P, T], F32, oX + 16 * K)
        RL = at("RL", [P, 2, T], F32, oX + 20 * K)
        MS = [at(f"MS{i}", [P, T], F32, oT[1 + i]) for i in range(2)]
        PP = [at(f"PP{i}", [P, T], F32, oT[3 + i]) for i in range(2)]
        PT = [at(f"PT{i}", [P, T], F32, [oKV, oKV + 4 * K][i]) for i in range(2)]

        UP = at("UP", [P, 4, S5L, NCH], F32, oX)
        US = at("US", [P, NG, NCH], F32, oX + 16 * K)
        S5P = at("S5P", [P, NPAR - NSMALL], F32, oR)
        CPR = at("CPR", [P, NPR, 9, GC], F32, oGX)
        CPI = at("CPI", [P, NPR, 9, GC], F32, oGX + 9216)
        WR = at("WR", [P, NPR, S5L, GC], F32, oGX + 18432)
        WI = at("WI", [P, NPR, S5L, GC], F32, oGX + 18432 + 8 * K)
        WTR = at("WTR", [P, NPR, P], F32, oX)
        WTI = at("WTI", [P, NPR, P], F32, oX + 8 * K)
        MM = at("MM", [P, NG, P], F32, oGX + 18432)
        KS = at("KS", [GC, NG, P], F32, oGX + 34816)
        GR = at("GR", [P, NPR, NCH], F32, oGX + 34816)
        GI = at("GI", [P, NPR, NCH], F32, oGX + 34816 + 8 * K)
        TM = at("TM", [P, NPR, NCH], F32, oGX + 51200)
        PW = at("PW", [P, 2, 9, NPR], F32, oGX + 59392)
        SV = at("SV", [P, 24, NPR], F32, oGX + 59392 + 1152)
        TBR = at("TBR", [P, NPR, NCH], F32, oT[1])
        TBI = at("TBI", [P, NPR, NCH], F32, oT[3])
        D0 = at("D0", [P, NPR, NCH], F32, oKV)
        HR = at("HR", [P, NPR, NCH], F32, oX)
        HI = at("HI", [P, NPR, NCH], F32, oX + 8 * K)
        YS = at("YS", [P, NG, NCH], F32, oGX + 34816)
        YT = at("YT", [P, 4, S5L, NCH], F32, oX)
        YB = at("YB", [P, 4, T], F32, oX + 16 * K)
        BBR = at("BBR", [P, NPR, GC], F32, oT[0])
        BBI = at("BBI", [P, NPR, GC], F32, oT[0] + 1024)
        BT = at("BT", [P, NPR, GC], F32, oT[0] + 2048)

        ME = at("ME", [P, KT, M], F32, oHID)
        MH = at("MH", [P, KT, M], R32, oHID + 8 * K)
        ML = at("ML", [P, KT, M], R32, oHID + 16 * K)
        MR = at("MR", [P, 2, M], F32, oHID + 24 * K)
        XKt = at("XKt", [P, XH, M], F32, oKV)
        XV = at("XV", [P, 2, XH * P], F32, oKV + 4 * K)
        XQ = at("XQ", [P, XH, T], F32, oT[1])
        OH = at("OH", [P, XH, T], R32, oHID)
        OL = at("OL", [P, XH, T], R32, oHID + 16 * K)
        XP = [at(f"XP{i}", [P, 4, M], F32, oGX + i * 4 * K) for i in range(2)]
        XT = [at(f"XT{i}", [P, 2, HALF], F32, oGX + 8 * K + i * 4 * K) for i in range(2)]

        PS = nc.alloc_psum_tensor("PS", [P, 8, HALF], F32)

        def acc(tile):
            b = 2 * (tile % 2)
            return PS[:, b:b + 2, :].rearrange("p a b -> p (a b)")

        def bank2(b):
            return PS[:, b:b + 2, :].rearrange("p a b -> p (a b)")

        def par(name, i=0, w=1):
            c = PCOLS[name]
            return PAR[:, c + i:c + i + w]

        UD = nc.dram_tensor("u_bounce", [NG, GC, S5L, NCH], F32, kind="Internal").ap()
        YD = nc.dram_tensor("y_bounce", [NG, GC, S5L, NCH], F32, kind="Internal").ap()

        mm = nc.tensor.matmul
        block = ctx.enter_context(nc.Block())

        @block.sync
        def _(sp):
            sp.dma_start(PAR[:], A["par"][:, 0:NSMALL]).then_inc(S("par_in"), 16)
            for k in range(KT):
                sp.dma_start(X[:, k, :], A["xT"][k * P:(k + 1) * P, :]).then_inc(S(f"x_in{k // 2}"), 16)
            sp.dma_start(WVR[:], A["wv"]).then_inc(S("wv_in"), 16)

            for i in range(RAW):
                sp.dma_start(RAWS[:, i, :, :], A["panels"][i]).then_inc(S(f"raw_full{i}"), 16)

            rounds = A["panels"].rearrange("(n r) p k m -> n r p k m", r=RAW)
            with sp.Fori(1, NPANEL // RAW) as i:
                for s in range(RAW):
                    sp.wait_ge(S("raw_free"), i * RAW + (s - (RAW - 1)))
                    sp.dma_start(RAWS[:, s, :, :],
                                 rounds[bass.ds(i, 1), s].rearrange("o p k m -> p (o k) m")
                                 ).then_inc(S(f"raw_full{s}"), 16)

        @block.gpsimd
        def _(pool):
            g = nc.gpsimd
            g.memset(ident[:], 0.0).then_inc(S("con"), 1)
            g.memset(ones[:], 1.0).then_inc(S("ones"), 1)
            g.memset(bones[:], 0.0).then_inc(S("con"), 1)
            g.memset(epsc[:, 0:1], EPS).then_inc(S("con"), 1)
            g.memset(epsc[:, 1:2], TWO_PI / 4).then_inc(S("con"), 1)
            g.memset(T0[:], 0.0).then_inc(S("con"), 1)
            pool.wait_ge(S("con"), 5)
            g.affine_select(out=ident[:], in_=ident[:], compare_op=ALU.not_equal, fill=1.0, base=0,
                            pattern=[[-1, P]], channel_multiplier=1).then_inc(S("con"), 1)
            for e in range(2):
                pool.wait_ge(S("con"), 6 + e)
                g.memset(bones[e * 64:(e + 1) * 64, e * 64:(e + 1) * 64], 1.0).then_inc(S("con"), 1)

            pool.wait_ge(S("con"), 8)
            pool.wait_ge(S("wv_in"), 16)
            g.tensor_copy(WVH[:], WVR[:]).then_inc(S("wv_hi"), 1)
            pool.wait_ge(S("wv_hi"), 1)
            g.tensor_tensor(WVL[:], WVR[:], WVH[:].bitcast(F32), ALU.subtract).then_inc(S("wv"), 1)

            def split(n, s):
                r = s % RAW
                g.tensor_copy(WH[:, s, :, :], RAWS[:, r, :, :]).then_inc(S("ws_hi"), 1)
                pool.wait_ge(S("ws_hi"), n + 1)
                g.tensor_tensor(WL[:, s, :, :], RAWS[:, r, :, :], WH[:, s, :, :].bitcast(F32),
                                ALU.subtract).then_inc(S("ws_full"), 1)
                pool.wait_ge(S("ws_full"), n + 1)
                pool.sem_inc(S("raw_free"), 1)

            for n in range(WSL):
                pool.wait_ge(S(f"raw_full{n % RAW}"), 16 * (n // RAW + 1))
                split(n, n)
            last = NPANEL - NPANEL % WSL
            with pool.Fori(WSL, last, WSL) as i:
                for s in range(WSL):
                    pool.wait_ge(S(f"raw_full{s % RAW}"), i * (16 // RAW) + 16 * (s // RAW + 1))
                    pool.wait_ge(S("ws_free"), i + (s - WSL + 1))
                    pool.sem_inc(S("split_begun"), 1)
                    split(i + s, s)
            for n in range(last, NPANEL):
                pool.wait_ge(S(f"raw_full{n % RAW}"), 16 * (n // RAW + 1))
                pool.wait_ge(S("ws_free"), n - WSL + 1)
                split(n, n % WSL)

        @block.tensor
        def _(pe):
            def open_panel(n, it=0):
                pe.wait_ge(S("ws_full"), it + (n + 1))

            def open_acc(t, it=0):
                if not (isinstance(it, int) and t + it < 2):
                    pe.wait_ge(S("acc_free"), it + (t - 1))

            def gemm(n, t, hi, lo, kt=KT, k0=0, ready=None, it=0, last=True):
                s = n % WSL
                a = acc(t)
                open_acc(t, it)
                for k in range(kt):
                    if ready:
                        ready(k)
                    for w, x, first in ((WH, hi, k == 0), (WH, lo, False), (WL, hi, False)):
                        for h in range(2):
                            ins = mm(a[:, h * HALF:(h + 1) * HALF], w[:, s, k0 + k, :],
                                     x[:, k, h * HALF:(h + 1) * HALF], start=first,
                                     stop=(w is WL and k == kt - 1))
                ins.then_inc(S("acc_full"), 1)
                return ins

            def done_panel():
                pe.sem_inc(S("ws_free"), 1)

            def norm_a(tag):
                pe.wait_ge(S("sq"), norm_base("sq", tag) + 1)
                for b in range(NBLK):
                    ins = mm(PS[:, 4, b:b + 1], SQ[:, b * P:(b + 1) * P], ones[:, 0:1], start=True, stop=True)
                ins.then_inc(S("na"), 1)

            def norm_b(tag):
                pe.wait_ge(S("diag"), norm_base("diag", tag) + 1)
                for h in range(2):
                    ins = mm(PS[:, 5 + h, :], ones[:], TT[4][:, h * HALF:(h + 1) * HALF], start=True, stop=True)
                ins.then_inc(S("nb"), 1)

            pe.sem_inc(S("used"), 1)
            pe.wait_ge(S("con"), 8)
            pe.wait_ge(S("ones"), 1)
            n0, t0 = PANEL0["in"], TILE0["in"]
            for m in range(12):
                open_panel(n0 + m)
                gemm(n0 + m, t0 + m, GH, GL,
                     ready=(lambda k: pe.wait_ge(S("gx"), k + 1)) if m == 0 else None)
                pe.wait_ge(S("acc_full"), t0 + m + 1)
                done_panel()
                if m == 0:
                    norm_a("mix0")
                if m == 1:
                    norm_b("mix0")
                if 1 <= m <= 4:
                    j = m - 1
                    pe.wait_ge(S("q_sq"), j + 1)
                    for b in range(NBLK):
                        ins = mm(PS[:, 7, b * 8 + 2 * j:b * 8 + 2 * j + 2], TT[2 + j % 2][:, b * P:(b + 1) * P],
                                 bones[:, 0:65:64], start=True, stop=True)
                    ins.then_inc(S("q_ms"), 1)
                if m == 5:
                    pe.wait_ge(S("k_sq"), 1)
                    for h in range(2):
                        ins = mm(PS[:, 5 + h, :], bones[:], TT[2][:, h * HALF:(h + 1) * HALF], start=True, stop=True)
                    ins.then_inc(S("k_ms"), 1)
            pe.wait_ge(S("wv"), 1)
            pe.wait_ge(S("k_rms"), 1)
            for b in range(NBLK):
                for k in range(KT):
                    for x, w in ((GH, WVH), (GL, WVH), (GH, WVL)):
                        ins = mm(PS[:, 5 + b // 4, (b % 4) * VW:(b % 4 + 1) * VW], x[:, k, b * P:(b + 1) * P],
                                 w[:, k, :], start=(k == 0 and w is WVH and x is GH),
                                 stop=(k == KT - 1 and w is WVL))
            ins.then_inc(S("vw_full"), 1)

            pe.wait_ge(S("w_ready"), 1)
            for i, src in enumerate((WR, WI)):
                for q in range(4):
                    b = 4 + q
                    if i == 1:
                        pe.wait_ge(S("wt_evac"), q + 1)
                    elif q == 0:
                        pe.wait_ge(S("v_evac"), 1)
                    for j in range(4):
                        ins = nc.tensor.transpose(PS[:, b, j * P:(j + 1) * P],
                                                  src[:, 4 * q + j, :, :].rearrange("p s c -> p (s c)"), ident[:])
                    ins.then_inc(S("wt_full"), 1)
            pe.wait_ge(S("cp_ready"), 1)
            for rnd in range(2):
                for q in range(4):
                    e, half = q // 2, q % 2
                    pe.wait_ge(S("wt_evac"), 5 + q) if rnd == 0 else pe.wait_ge(S("ks_evac"), q + 1)
                    for j in range(4):
                        pr = rnd * 8 + half * 4 + j
                        rows = slice(e * 64, e * 64 + 64)
                        for i, (bb, cp) in enumerate(((BBR, CPR), (BBI, CPI))):
                            ins = mm(PS[0:GC, 4 + q, j * P:(j + 1) * P], bb[rows, pr, :],
                                     cp[rows, pr, 0:8, :].rearrange("p t c -> p (t c)"),
                                     start=(i == 0), stop=(i == 1))
                    ins.then_inc(S("ks_full"), 1)
            pe.wait_ge(S("us_in"), 8 * 16)
            for i, wt in enumerate((WTR, WTI)):
                for q in range(4):
                    b = 4 + q
                    if i == 0:
                        pe.wait_ge(S("ks_evac"), 5 + q)
                    for j in range(4):
                        pr = 4 * q + j
                        for e in range(2):
                            ins = mm(PS[e * 64:(e + 1) * 64, (0 if i else 4) + q, j * P:(j + 1) * P],
                                     wt[:, pr, e * 64:(e + 1) * 64], US[:, 2 * pr + e, :], start=True, stop=True)
                ins.then_inc(S("bu_full"), 1)
            pe.wait_ge(S("mm_in"), 8 * 16)
            pe.wait_ge(S("h_ready"), 1)
            for rnd in range(2):
                for q in range(4):
                    e, half = q // 2, q % 2
                    if rnd == 1:
                        pe.wait_ge(S("ys_evac"), q + 1)
                    for j in range(4):
                        pr = rnd * 8 + half * 4 + j
                        gidx = 2 * pr + e
                        rows = slice(e * 64, e * 64 + 64)
                        mm(PS[:, 4 + q, j * P:(j + 1) * P], MM[:, gidx, :], US[:, gidx, :], start=True, stop=False)
                        for i, (cp, hh) in enumerate(((CPR, HR), (CPI, HI))):
                            ins = mm(PS[:, 4 + q, j * P + 1:(j + 1) * P],
                                     cp[rows, pr, 1:9, :].rearrange("p t c -> p (t c)"),
                                     hh[rows, pr, 0:NCH - 1], start=False, stop=(i == 1))
                    ins.then_inc(S("ys_full"), 1)
            n0, t0 = PANEL0["glu"], TILE0["glu"]
            pe.wait_ge(S("yb_split"), 4)
            for m in range(4):
                if m % 2 == 0:
                    open_panel(n0 + m // 2)
                gemm(n0 + m // 2, t0 + m, GH, GL, kt=4, k0=4 * (m % 2))
                if m % 2:
                    pe.wait_ge(S("acc_full"), t0 + m + 1)
                    done_panel()
            pe.wait_ge(S("acc_free"), t0 + 4)

            for b in range(NBLK):
                n = (b + 1) * P
                qs = slice(b * P, n)
                if n > TOPK:
                    for h in range(IH):
                        rows = slice((h % 2) * 64, (h % 2) * 64 + 64)
                        ib = (b - 2) * IH + h
                        bk = 4 + 2 * (h % 2)
                        if b == 2 and h < 2:
                            pe.wait_ge(S("ms_full"), AH * b - 1 + h)
                        elif ib >= 2 and h < 2:
                            pe.wait_ge(S("ms_full"), AH * b - 1 + h)
                        else:
                            pe.wait_ge(S("rl"), ib - 1)
                        for c in range(0, n, HALF):
                            w = min(HALF, n - c)
                            ins = mm(PS[:, bk + c // HALF, 0:w], IQ[rows, h // 2, qs], IK[rows, c:c + w],
                                     start=True, stop=True)
                        ins.then_inc(S("ix_full"), 1)

                def scores(h):
                    i = b * AH + h
                    rows = slice((h % 2) * 64, (h % 2) * 64 + 64)
                    bk = 4 + 2 * (h % 2)
                    if h < 2 and n > TOPK:
                        pe.wait_ge(S("rl"), (b - 2) * IH + 3 + h)
                    elif i >= 2:
                        pe.wait_ge(S("ms_full"), i - 1)
                    for c in range(0, n, HALF):
                        w = min(HALF, n - c)
                        ins = mm(PS[:, bk + c // HALF, 0:w], Q[rows, h // 2, qs], KK[rows, c:c + w],
                                 start=True, stop=True)
                    ins.then_inc(S("s_full"), 1)

                def turn(h):
                    i = b * AH + h
                    pe.wait_ge(S("p_ready"), i + 1)
                    if i:
                        pe.wait_ge(S("pt_ready"), i)
                    for c in range(b + 1):
                        ins = nc.tensor.transpose(PS[:, c // 4, (c % 4) * P:(c % 4 + 1) * P],
                                                  PP[i % 2][:, c * P:(c + 1) * P], ident[:])
                    ins.then_inc(S("t_full"), 1)

                def weigh(h):
                    i = b * AH + h
                    pe.wait_ge(S("pt_ready"), i + 1)
                    if h == 0 and b >= 2:
                        pe.wait_ge(S("ya"), b - 1)
                    for c in range(b + 1):
                        ins = mm(PS[(h % 2) * 64:(h % 2) * 64 + 64, 2 + b % 2, (h // 2) * P:(h // 2 + 1) * P],
                                 VV[:, c, 0:AD], PT[i % 2][:, c * P:(c + 1) * P], start=(c == 0), stop=(c == b))
                    ins.then_inc(S("o_full"), 1)

                scores(0)
                scores(1)
                for h in range(AH):
                    turn(h)
                    if h + 2 < AH:
                        scores(h + 2)
                    weigh(h)

            n0, t0 = PANEL0["out"], TILE0["out"]
            pe.wait_ge(S("ya"), NBLK)
            pe.wait_ge(S("yb"), 4)
            for m in range(8):
                open_panel(n0 + m)
                gemm(n0 + m, t0 + m, GH, GL)
                pe.wait_ge(S("acc_full"), t0 + m + 1)
                done_panel()

            def grouped(tag, nup, ngrp):
                n0, t0 = PANEL0[tag], TILE0[tag]
                per = nup + 2
                tper = nup + 8
                dn = S("hid")

                def up(n, t, first=False, it=0, tit=0):
                    for j in range(nup):
                        open_panel(n + j, it)
                        gemm(n + j, t + j, GH, GL, it=tit,
                             ready=(lambda k: pe.wait_ge(S("gx"), norm_base("gx", GROUPED_NORM[tag]) + k + 1)) if first and j == 0 else None)
                        pe.wait_ge(S("acc_full"), tit + (t + j + 1))
                        done_panel()
                        if first and j == 0:
                            norm_a(GROUPED_NORM[tag])
                        if first and j == 1:
                            norm_b(GROUPED_NORM[tag])

                def down(n, t, buf, hid, it=0, tit=0, hit=0):
                    pe.wait_ge(dn, grouped_base("hid", tag) + hit + hid)
                    for j in range(8):
                        if j % 4 == 0:
                            open_panel(n + j // 4, it)
                        gemm(n + j // 4, t + j, HH[:, 2 * buf:2 * buf + 2, :], HL[:, 2 * buf:2 * buf + 2, :],
                             kt=2, k0=2 * (j % 4), it=tit)
                        if j % 4 == 3:
                            pe.wait_ge(S("acc_full"), tit + (t + j + 1))
                            done_panel()
                    pe.sem_inc(S("used"), 1)

                up(n0, t0, first=True)
                pairs = (ngrp - 1) // 2
                n1, t1 = n0 + nup, t0 + nup
                if pairs > 1:
                    with pe.Fori(0, pairs) as i:
                        it, tit = i * (2 * per), i * (2 * tper)
                        hit = i * (2 * GRP)
                        up(n1, t1, it=it, tit=tit)
                        down(n1 + nup, t1 + nup, 0, GRP, it, tit, hit)
                        up(n1 + per, t1 + tper, it=it, tit=tit)
                        down(n1 + per + nup, t1 + tper + nup, 1, 2 * GRP, it, tit, hit)
                    g = 2 * pairs
                    n1, t1 = n1 + g * per, t1 + g * tper
                else:
                    g = 0
                while g < ngrp - 1:
                    up(n1, t1)
                    down(n1 + nup, t1 + nup, g % 2, GRP * (g + 1))
                    n1, t1 = n1 + per, t1 + tper
                    g += 1
                down(n1, t1, g % 2, GRP * (g + 1))

            def cross(l):
                n0, t0 = PANEL0[f"xk{l}"], TILE0[f"xk{l}"]
                pe.wait_ge(S("me_sq"), 1 * l + 1)
                ins = mm(PS[:, 7, 0:M], ones[:], MR[:, 0, :], start=True, stop=True)
                ins.then_inc(S("me_ss"), 1)
                pe.wait_ge(S("me_split"), 8 * l + KT)
                for m in range(4):
                    open_panel(n0 + m)
                    open_acc(t0 + m)
                    a = acc(t0 + m)
                    s = (n0 + m) % WSL
                    for k in range(KT):
                        for w, x in ((WH, MH), (WH, ML), (WL, MH)):
                            ins = mm(a[:, 0:M], w[:, s, k, :], x[:, k, :], start=(k == 0 and w is WH and x is MH),
                                     stop=(k == KT - 1 and w is WL))
                    ins.then_inc(S("acc_full"), 1)
                    pe.wait_ge(S("acc_full"), t0 + m + 1)
                    done_panel()
                n0, t0 = PANEL0[f"xv{l}"], TILE0[f"xv{l}"]
                open_acc(t0)
                a = acc(t0)
                for m in range(4):
                    open_panel(n0 + m)
                    s = (n0 + m) % WSL
                    for kk in range(2):
                        k = 2 * m + kk
                        for x, w in ((MH, WH), (ML, WH), (MH, WL)):
                            for c in range(2):
                                ins = mm(a[:, c * HALF:(c + 1) * HALF], x[:, k, c * P:(c + 1) * P],
                                         w[:, s, 4 * kk:4 * kk + 4, :].rearrange("p a b -> p (a b)"),
                                         start=(k == 0 and w is WH and x is MH), stop=(k == KT - 1 and w is WL))
                    if m < 3:
                        ins.then_inc(S("xv_part"), 1)
                        pe.wait_ge(S("xv_part"), 3 * l + m + 1)
                        done_panel()
                ins.then_inc(S("acc_full"), 1)
                pe.wait_ge(S("acc_full"), t0 + 1)
                done_panel()
                pe.wait_ge(S("xk_sq"), 1 * l + 1)
                for h in range(2):
                    ins = mm(PS[:, 5 + h, :], ones[:], TT[4][:, h * HALF:(h + 1) * HALF], start=True, stop=True)
                ins.then_inc(S("xk_ms"), 1)
                n0, t0 = PANEL0[f"xq{l}"], TILE0[f"xq{l}"]
                for m in range(4):
                    open_panel(n0 + m)
                    gemm(n0 + m, t0 + m, GH, GL,
                         ready=(lambda k: pe.wait_ge(S("gx"), norm_base("gx", f"x{l}") + k + 1)) if m == 0 else None)
                    pe.wait_ge(S("acc_full"), t0 + m + 1)
                    done_panel()
                    if m == 0:
                        pe.wait_ge(S("xk_rms"), 1 * l + 1)
                        norm_a(f"x{l}")
                for m in range(4):
                    pe.wait_ge(S("xq_sq"), 4 * l + m + 1)
                    for b in range(NBLK):
                        ins = mm(PS[:, 7, b * 4 + m:b * 4 + m + 1], R[:, b * P:(b + 1) * P] if m % 2 else
                                 T0[:, b * P:(b + 1) * P], ones[:, 0:1], start=True, stop=True)
                    ins.then_inc(S("xq_ms"), 1)
                pe.wait_ge(S("xk_ready"), 1 * l + 1)
                for b in range(NBLK):
                    if b >= 1:
                        pe.wait_ge(S("xs_read"), 8 * l + b)
                    else:
                        pe.wait_ge(S("xfq"), 1 * l + 1)
                    for h in range(XH):
                        ins = mm(PS[:, 4 + h // 2, (h % 2) * M:(h % 2 + 1) * M], XQ[:, h, b * P:(b + 1) * P],
                                 XKt[:, h, :], start=True, stop=True)
                    ins.then_inc(S("xs_full"), 1)
                    pe.wait_ge(S("xp"), 8 * l + b + 1)
                    if b >= 1:
                        pe.wait_ge(S("xt"), 8 * l + b)
                    for c in range(2):
                        for h in range(XH):
                            ins = nc.tensor.transpose(PS[:, 6 + c, h * P:(h + 1) * P],
                                                      XP[b % 2][:, h, c * P:(c + 1) * P], ident[:])
                    ins.then_inc(S("xt_full"), 1)
                    pe.wait_ge(S("xt"), 8 * l + b + 1)
                    if b >= 2:
                        pe.wait_ge(S("xo_evac"), 8 * l + b - 1)
                    else:
                        pe.wait_ge(S("acc_free"), TILE0[f"xq{l}"] + 4)
                    for h in range(XH):
                        for c in range(2):
                            ins = mm(PS[:, b % 2, h * P:(h + 1) * P], XV[:, c, h * P:(h + 1) * P],
                                     XT[b % 2][:, c, h * P:(h + 1) * P], start=(c == 0), stop=(c == 1))
                    ins.then_inc(S("xo_full"), 1)
                n0, t0 = PANEL0[f"xo{l}"], TILE0[f"xo{l}"]
                pe.wait_ge(S("xo_evac"), 8 * l + NBLK)
                for m in range(8):
                    if m % 2 == 0:
                        open_panel(n0 + m // 2)
                    gemm(n0 + m // 2, t0 + m, OH, OL, kt=4, k0=4 * (m % 2))
                    if m % 2:
                        pe.wait_ge(S("acc_full"), t0 + m + 1)
                        done_panel()

            cross(0)
            grouped("mlp0", 4, NGRP)
            grouped("odd", 6, OGRP)
            cross(1)
            grouped("mlp1", 4, NGRP)

        @block.scalar
        def _(act):
            a = nc.scalar

            def gx(tag, k, n=None):
                act.wait_ge(S("x"), norm_base("x", tag) + k + 1) if tag != "mix0" else act.wait_ge(S(f"x_in{k // 2}"), 32)
                if k == 0 and tag == "mix0":
                    act.wait_ge(S("par_in"), 16)
                a.activation(GH[:, k, :], X[:, k, :], ACT.Copy, scale=par(tag, k)).then_inc(S("gh"), 1)
                if k == 0:
                    a.activation(SQ[:], X[:, k, :], ACT.Square).then_inc(S("sqt"), 1)
                else:
                    if k >= 3:
                        act.wait_ge(S("sqa"), norm_base("sqa", tag) + k - 2)
                    a.activation(TT[2 + k % 2][:], X[:, k, :], ACT.Square).then_inc(S("sqt"), 1)

            def norm(tag, both=True):
                act.wait_ge(S("na"), norm_base("na", tag) + 1)
                act.wait_ge(S("con"), 8)
                a.activation(rTa[:], PS[:, 4, 0:NBLK], ACT.Sqrt, bias=epsc[:, 0:1], scale=1.0 / D).then_inc(S("rta"), 1)
                if both:
                    act.wait_ge(S("nb"), norm_base("nb", tag) + 1)
                    a.activation(R[:], bank2(5), ACT.Copy).then_inc(S("R"), 1)

            for k in range(KT):
                gx("mix0", k)
            norm("mix0")
            for j in range(4):
                act.wait_ge(S("q_copy"), j + 1)
                if j >= 2:
                    act.wait_ge(S("q_ms"), j - 1)
                else:
                    act.wait_ge(S("sqa"), KT - 1)
                a.activation(TT[2 + j % 2][:], Q[:, j, :], ACT.Square).then_inc(S("q_sq"), 1)
            act.wait_ge(S("k_copy"), 1)
            act.wait_ge(S("q_ms"), 4)
            a.activation(TT[2][:], KK[:], ACT.Square).then_inc(S("k_sq"), 1)
            act.wait_ge(S("k_ms"), 1)
            a.activation(TT[3][:], bank2(5), ACT.Sqrt, bias=epsc[:, 0:1], scale=1.0 / AD).then_inc(S("k_rms"), 1)
            act.wait_ge(S("q_var"), 1)
            a.activation(fqa[:], fq[:], ACT.Sqrt, bias=epsc[:, 0:1], scale=1.0 / AD).then_inc(S("q_rms"), 1)

            act.wait_ge(S("u_evac"), 4)
            act.dma_start(S5P[:], A["par"][:, NSMALL:NPAR]).then_inc(S("s5p"), 16)
            act.dma_start(UD.rearrange("(a g) c s j -> (g c) a s j", a=4), UP[:]).then_inc(S("u_out"), 16)
            act.wait_ge(S("u_out"), 16)
            for s in range(S5L):
                act.dma_start(US[s * GC:(s + 1) * GC, :, :], UD[:, :, s, :].rearrange("g c j -> c g j")).then_inc(S("us_in"), 16)
            act.wait_ge(S("s5p"), 16)
            act.wait_ge(S("v_evac"), 1)
            o = PCOLS["lstep"] - NSMALL
            a.activation(SV[:, 0, :], S5P[:, o:o + NPR], ACT.Exp).then_inc(S("delta"), 1)
            act.wait_ge(S("logmag"), 1)
            a.activation(SV[:, 3, :], SV[:, 1, :], ACT.Exp).then_inc(S("mag"), 1)
            a.activation(SV[:, 4, :], SV[:, 1, :], ACT.Exp, scale=float(S5L)).then_inc(S("mag"), 1)
            act.wait_ge(S("angle"), 1)
            a.activation(SV[:, 8, :], SV[:, 5, :], ACT.Sin).then_inc(S("sincos"), 1)
            a.activation(SV[:, 9, :], SV[:, 7, :], ACT.Sin).then_inc(S("sincos"), 1)
            act.wait_ge(S("us_in"), 8 * 16)
            for i, dst in enumerate((WTR, WTI)):
                for q in range(4):
                    act.wait_ge(S("wt_full"), 4 * i + q + 1)
                    a.activation(dst[:, 4 * q:4 * q + 4, :].rearrange("p a b -> p (a b)"), PS[:, 4 + q, :],
                                 ACT.Copy).then_inc(S("wt_evac"), 1)
            for i in range(8):
                rnd, q = i // 4, i % 4
                e, half = q // 2, q % 2
                act.wait_ge(S("ks_full"), i + 1)
                pr = rnd * 8 + half * 4
                dst = KS[:, 2 * pr:2 * pr + 8, :].rearrange("p (a e) b -> p e a b", e=2)[:, e]
                a.activation(dst, PS[0:GC, 4 + q, :].rearrange("p (a b) -> p a b", a=4), ACT.Copy).then_inc(S("ks_evac"), 1)
            act.wait_ge(S("ks_d"), 1)
            act.wait_ge(S("mm_zero"), 1)
            for s in range(S5L):
                act.dma_start(MM[s * GC:(s + 1) * GC, :, s * GC:P], KS[:, :, 0:P - s * GC]).then_inc(S("mm_in"), 16)
            for i in range(8):
                rnd, q = i // 4, i % 4
                e, half = q // 2, q % 2
                act.wait_ge(S("ys_full"), i + 1)
                pr = rnd * 8 + half * 4
                dst = YS[:, 2 * pr:2 * pr + 8, :].rearrange("p (a e) b -> p e a b", e=2)[:, e]
                a.activation(dst, PS[:, 4 + q, :].rearrange("p (a b) -> p a b", a=4), ACT.Copy).then_inc(S("ys_evac"), 1)
            act.wait_ge(S("ys_evac"), 8)
            for s in range(S5L):
                act.dma_start(YD[:, :, s, :].rearrange("g c j -> c g j"), YS[s * GC:(s + 1) * GC, :, :]).then_inc(S("y_out"), 16)
            act.wait_ge(S("y_out"), 8 * 16)
            act.dma_start(YT[:], YD.rearrange("(a g) c s j -> (g c) a s j", a=4)).then_inc(S("yt_in"), 16)
            act.wait_ge(S("yt_in"), 16)
            for m in range(4):
                a.activation(YB[:, m, :].rearrange("p (j s) -> p s j", s=S5L), YT[:, m, :, :],
                             ACT.Gelu_apprx_tanh).then_inc(S("yb_gelu"), 1)
                act.wait_ge(S("yb_gelu"), m + 1)
                a.activation(GH[:, m, :], YB[:, m, :], ACT.Copy).then_inc(S("yb_hi"), 1)
            for m in range(4):
                act.wait_ge(S("glu_evac"), m + 1)
                a.activation(TT[1 + m % 2][:], TT[1 + m % 2][:], ACT.Sigmoid, bias=par("bglu", m)).then_inc(S("glu_sig"), 1)
                act.wait_ge(S("glu_z"), m + 1)
                a.activation(GH[:, 4 + m, :], TT[1 + m % 2][:], ACT.Copy).then_inc(S("z_hi"), 1)

            for b in range(NBLK):
                n = (b + 1) * P
                if n > TOPK:
                    for h in range(IH):
                        ib = (b - 2) * IH + h
                        act.wait_ge(S("ix_full"), ib + 1)
                        if ib >= 2:
                            act.wait_ge(S("sc"), ib - 1)
                        a.activation(RL[:, h % 2, 0:n], bank2(4 + 2 * (h % 2))[:, 0:n], ACT.Relu).then_inc(S("rl"), 1)
                for h in range(AH):
                    i = b * AH + h
                    act.wait_ge(S("nmax"), i + 1)
                    if i >= 2:
                        act.wait_ge(S("t_full"), i - 1)
                    a.activation(PP[i % 2][:, 0:n], MS[i % 2][:, 0:n], ACT.Exp, bias=sm1[:, 2 + i % 2:3 + i % 2],
                                 scale=fq[:, b * 8 + h:b * 8 + h + 1],
                                 accum_out=sm1[:, 4 + i % 2:5 + i % 2]).then_inc(S("p_exp"), 1)
                    act.wait_ge(S("t_full"), i + 1)
                    if i >= 2:
                        act.wait_ge(S("o_full"), i - 1)
                    a.activation(PT[i % 2][:, 0:n], bank2(0)[:, 0:n], ACT.Copy).then_inc(S("pt_ready"), 1)
                act.wait_ge(S("o_full"), (b + 1) * AH)
                a.activation(GH[:, 0:4, b * P:(b + 1) * P], PS[:, 2 + b % 2, :].rearrange("p (a b) -> p a b", a=4),
                             ACT.Copy).then_inc(S("ya_hi"), 1)

            def cross(l):
                act.wait_ge(S("me_free"), 1 * l + 1)
                act.dma_start(ME[:], A["memT"].rearrange("(k p) m -> p k m", p=P)).then_inc(S("me_in"), 16)
                act.wait_ge(S("me_ss"), 1 * l + 1)
                a.activation(MR[:, 1, :], PS[:, 7, 0:M], ACT.Sqrt, bias=epsc[:, 0:1], scale=1.0 / D).then_inc(S("me_rms"), 1)
                for k in range(KT):
                    act.wait_ge(S("me_n"), 8 * l + k + 1)
                    a.activation(MH[:, k, :], ME[:, k, :], ACT.Copy).then_inc(S("mh"), 1)
                act.wait_ge(S("xk_raw"), 1 * l + 1)
                a.activation(TT[4][:], XKt[:].rearrange("p a b -> p (a b)"), ACT.Square).then_inc(S("xk_sq"), 1)
                act.wait_ge(S("xk_ms"), 1 * l + 1)
                a.activation(TT[3][:], bank2(5), ACT.Sqrt, bias=epsc[:, 0:1], scale=1.0 / P).then_inc(S("xk_rms"), 1)
                norm(f"x{l}", both=False)
                for m in range(4):
                    act.wait_ge(S("xq_copy"), 4 * l + m + 1)
                    if m >= 2:
                        act.wait_ge(S("xq_ms"), 4 * l + m - 1)
                    dst = R[:] if m % 2 else T0[:, 0:T]
                    a.activation(dst, XQ[:, m, :], ACT.Square).then_inc(S("xq_sq"), 1)
                act.wait_ge(S("xq_var"), 1 * l + 1)
                a.activation(fqa[:, 0:32], fq[:, 0:32], ACT.Sqrt, bias=epsc[:, 0:1], scale=1.0 / P).then_inc(S("xq_rms"), 1)
                for b in range(NBLK):
                    act.wait_ge(S("xnmax"), 8 * l + b + 1)
                    if b >= 2:
                        act.wait_ge(S("xt_full"), 8 * l + b - 1)
                    for h in range(XH):
                        ins = a.activation(XP[b % 2][:, h, :], PS[:, 4 + h // 2, (h % 2) * M:(h % 2 + 1) * M], ACT.Exp,
                                           bias=sm1[:, h:h + 1], scale=fq[:, b * 4 + h:b * 4 + h + 1],
                                           accum_out=sm2[:, h:h + 1])
                    ins.then_inc(S("xp_exp"), 1)
                    act.wait_ge(S("xt_full"), 8 * l + b + 1)
                    if b >= 2:
                        act.wait_ge(S("xo_full"), 8 * l + b - 1)
                    a.activation(XT[b % 2][:].rearrange("p a b -> p (a b)"), bank2(6), ACT.Copy).then_inc(S("xt"), 1)
                    act.wait_ge(S("xo_full"), 8 * l + b + 1)
                    a.activation(OH[:, :, b * P:(b + 1) * P], PS[:, b % 2, :].rearrange("p (a b) -> p a b", a=4),
                                 ACT.Copy).then_inc(S("oh"), 1)
                for k in range(KT):
                    gx(f"ffn{l}", k)

            def grouped(tag, l, ngrp, nxt):
                hid = S("hh")
                norm(GROUPED_NORM[tag])

                def tile(f, cnt, j, it=0):
                    c = it + cnt
                    if tag == "odd":
                        w2, bias = par("ocw", 16 + f), par("ocb", f)
                    else:
                        c0, c1 = PCOLS[f"fcw{l}"] + 2 * FT, PCOLS[f"fcb{l}"]
                        if isinstance(f, int):
                            w2, bias = PAR[:, c0 + f:c0 + f + 1], PAR[:, c1 + f:c1 + f + 1]
                        else:
                            w2, bias = PAR[:, bass.ds(f + c0, 1)], PAR[:, bass.ds(f + c1, 1)]
                    act.wait_ge(S("sig"), grouped_base("sig", tag) + c + 1)
                    a.activation(TT[1][:], T0[:, 2:T + 2], ACT.Identity, bias=bias, scale=w2).then_inc(S("tap"), 1)
                    if tag != "odd":
                        act.wait_ge(S("conv"), grouped_base("conv", tag) + c + 1)
                        a.activation(TT[1][:], TT[1][:], ACT.Silu).then_inc(S("act"), 1)
                    act.wait_ge(S("h"), grouped_base("h", tag) + c + 1)
                    a.activation(HH[:, j, :], TT[2][:], ACT.Copy).then_inc(hid, 1)

                for j in range(GRP):
                    tile(j, j, j)
                pairs = (ngrp - 1) // 2
                if pairs > 1:
                    with act.Fori(0, pairs) as i:
                        it = i * (2 * GRP)
                        for j in range(2 * GRP):
                            tile(it + (GRP + j), GRP + j, (GRP + j) % (2 * GRP), it)
                    f = GRP + pairs * 2 * GRP
                else:
                    f = GRP
                while f < ngrp * GRP:
                    tile(f, f, f % (2 * GRP))
                    f += 1
                if nxt:
                    for k in range(KT):
                        gx(nxt, k)

            act.wait_ge(S("x_free"), 1)
            act.dma_start(X[:], A["xT"].rearrange("(k p) t -> p k t", p=P)).then_inc(S("x_back"), 16)
            for k in range(KT):
                gx("x0", k)
            cross(0)
            grouped("mlp0", 0, NGRP, "mix1")
            grouped("odd", 1, OGRP, "x1")
            cross(1)
            grouped("mlp1", 1, NGRP, None)
            for k in range(KT):
                act.wait_ge(S("x"), norm_base("x", "end") + k + 1)
                act.dma_start(A["outT"][k * P:(k + 1) * P, :], X[:, k, :]).then_inc(S("stored"), 16)
            act.wait_ge(S("stored"), 16 * KT)
            act.wait_ge(S("u_out"), 16)
            act.wait_ge(S("y_out"), 8 * 16)

        @block.vector
        def _(dve):
            v = nc.vector
            chain = [0]

            def link(ins):
                chain[0] += 1
                ins.then_inc(S("dve_chain"), 1)
                dve.wait_ge(S("dve_chain"), chain[0])

            def also(ins, sem, n=1):
                ins.then_inc(S(sem), n)

            def gxlo(tag, k):
                dve.wait_ge(S("gh"), norm_base("gh", tag) + k + 1)
                v.scalar_tensor_tensor(GL[:, k, :], X[:, k, :], par(tag, k), GH[:, k, :].bitcast(F32),
                                       ALU.mult, ALU.subtract).then_inc(S("gx"), 1)
                dve.wait_ge(S("sqt"), norm_base("sqt", tag) + k + 1)
                if k:
                    if k > 1:
                        dve.wait_ge(S("sqa"), norm_base("sqa", tag) + k - 1)
                    v.tensor_tensor(SQ[:], SQ[:], TT[2 + k % 2][:], ALU.add).then_inc(S("sqa"), 1)

            def norm(tag, both=True):
                dve.wait_ge(S("rta"), norm_base("rta", tag) + 1)
                v.reciprocal(rT[:], rTa[:]).then_inc(S("rt"), 1)
                dve.wait_ge(S("rt"), norm_base("rt", tag) + 1)
                if both:
                    d = TT[4][:].rearrange("p (b t) -> p b t", b=NBLK)
                    v.tensor_tensor(d, ident[:].rearrange("p (o t) -> p o t", o=1).broadcast_to([P, NBLK, P]),
                                    rT[:].rearrange("p (b o) -> p b o", o=1).broadcast_to([P, NBLK, P]),
                                    ALU.mult).then_inc(S("diag"), 1)

            def sq_done(tag):
                dve.wait_ge(S("sqa"), norm_base("sqa", tag) + KT - 1)
                dve.sem_inc(S("sq"), 1)

            dve.wait_ge(S("par_in"), 16)
            for k in range(KT):
                gxlo("mix0", k)
            sq_done("mix0")
            dve.wait_ge(S("con"), 8)
            norm("mix0")
            dve.wait_ge(S("R"), 1)

            def evac(t, it=0):
                dve.wait_ge(S("acc_full"), it + (t + 1))
                return acc(t)

            t0 = TILE0["in"]
            for m in range(4):
                p = evac(t0 + m)
                ins = v.tensor_copy(Q[:, m, :], p)
                ins.then_inc(S("q_copy"), 1)
                dve.wait_ge(S("q_copy"), m + 1)
                dve.sem_inc(S("acc_free"), 1)
            p = evac(t0 + 4)
            v.tensor_tensor(KK[:], p, R[:], ALU.mult).then_inc(S("k_copy"), 1)
            dve.wait_ge(S("k_copy"), 1)
            dve.sem_inc(S("acc_free"), 1)
            for m in range(2):
                p = evac(t0 + 5 + m)
                v.tensor_copy(IQ[:, m, :], p).then_inc(S("acc_free"), 1)
            p = evac(t0 + 7)
            v.tensor_tensor(IK[:], p, R[:], ALU.mult).then_inc(S("acc_free"), 1)
            dve.wait_ge(S("q_ms"), 4)
            r2 = rTa
            link(v.tensor_tensor(r2[:], rT[:], rT[:], ALU.mult))
            bc = lambda x: x[:].rearrange("p (b o) -> p b o", o=1).broadcast_to([P, NBLK, AH])
            f3 = lambda x: x[:].rearrange("p (b h) -> p b h", h=AH)
            v.tensor_tensor(f3(fq), PS[:, 7, 0:64].rearrange("p (b h) -> p b h", h=AH), bc(r2), ALU.mult).then_inc(S("q_var"), 1)
            dve.wait_ge(S("k_rms"), 1)
            v.reciprocal(TT[2][:], TT[3][:]).then_inc(S("k_r"), 1)
            link(v.tensor_tensor(sm1[:, 0:1], par("aq"), par("ak"), ALU.mult))
            dve.wait_ge(S("k_r"), 1)
            link(v.scalar_tensor_tensor(KK[:], KK[:], sm1[:, 0:1], TT[2][:], ALU.mult, ALU.mult))
            dve.wait_ge(S("q_rms"), 1)
            link(v.reciprocal(fqa[:], fqa[:]))
            link(v.scalar_tensor_tensor(f3(fq), f3(fqa), AD ** -0.5, bc(rT), ALU.mult, ALU.mult))
            for m in range(4):
                p = evac(t0 + 8 + m)
                v.tensor_tensor(UP[:, m, :, :].rearrange("p s j -> p j s"), p.rearrange("p (j s) -> p j s", s=S5L),
                                R[:].rearrange("p (j s) -> p j s", s=S5L), ALU.mult).then_inc(S("u_evac"), 1)
                dve.wait_ge(S("u_evac"), m + 1)
                dve.sem_inc(S("acc_free"), 1)
            dve.wait_ge(S("vw_full"), 1)
            for b in range(NBLK):
                ins = v.tensor_scalar(VV[:, b, :], PS[:, 5 + b // 4, (b % 4) * VW:(b % 4 + 1) * VW], rT[:, b:b + 1], None, ALU.mult)
                ins.then_inc(S("vv"), 1)
            dve.wait_ge(S("vv"), NBLK)
            dve.sem_inc(S("v_evac"), 1)

            dve.wait_ge(S("s5p"), 16)
            sp_ = lambda nm, w: S5P[:, PCOLS[nm] - NSMALL:PCOLS[nm] - NSMALL + w]
            lre, lim = sp_("lre", NPR), sp_("lim", NPR)
            sv = lambda i: SV[:, i, :]
            mul = lambda o, x, y: link(v.tensor_tensor(o, x, y, ALU.mult))
            add = lambda o, x, y: link(v.tensor_tensor(o, x, y, ALU.add))
            sub = lambda o, x, y: link(v.tensor_tensor(o, x, y, ALU.subtract))
            dve.wait_ge(S("delta"), 1)
            v.tensor_tensor(sv(1), lre, sv(0), ALU.mult).then_inc(S("logmag"), 1)
            mul(sv(2), lim, sv(0))
            link(v.tensor_scalar(sv(6), sv(2), 1.0 / TWO_PI, 12582912.0, ALU.mult, ALU.add))
            link(v.tensor_scalar(sv(6), sv(6), -12582912.0, None, ALU.add))
            link(v.scalar_tensor_tensor(sv(5), sv(6), -PI_A, sv(2), ALU.mult, ALU.add))
            link(v.scalar_tensor_tensor(sv(5), sv(6), -PI_B, sv(5), ALU.mult, ALU.add))
            link(v.scalar_tensor_tensor(sv(5), sv(6), -PI_C, sv(5), ALU.mult, ALU.add))
            link(v.tensor_scalar(sv(5), sv(5), 3.1415925, -3.1415925, ALU.min, ALU.max))
            link(v.tensor_scalar(sv(7), sv(5), -1.0, None, ALU.mult))
            link(v.tensor_tensor(sv(7), sv(7), sv(5), ALU.max))
            v.tensor_scalar(sv(7), sv(7), -1.0, TWO_PI / 4, ALU.mult, ALU.add).then_inc(S("angle"), 1)
            dve.wait_ge(S("mag"), 2)
            dve.wait_ge(S("sincos"), 2)
            cos, sin = sv(9), sv(8)
            pr_, pi_ = PW[:, 0], PW[:, 1]
            link(v.memset(pr_[:, 0, :], 1.0))
            link(v.memset(pi_[:, 0, :], 0.0))
            mul(pr_[:, 1, :], sv(3), cos)
            mul(pi_[:, 1, :], sv(3), sin)
            link(v.tensor_scalar(sv(10), pr_[:, 1, :], -1.0, None, ALU.add))
            mul(sv(11), lre, lre)
            mul(sv(12), lim, lim)
            add(sv(11), sv(11), sv(12))
            link(v.reciprocal(sv(11), sv(11)))
            mul(sv(12), sv(10), lre)
            mul(sv(13), pi_[:, 1, :], lim)
            add(sv(12), sv(12), sv(13))
            mul(sv(12), sv(12), sv(11))
            mul(sv(13), pi_[:, 1, :], lre)
            mul(sv(14), sv(10), lim)
            sub(sv(13), sv(13), sv(14))
            mul(sv(13), sv(13), sv(11))

            def cmul(orr, oi, ar, ai, br, bi, t, neg=False):
                mul(t, ai, bi)
                mul(orr, ar, br)
                sub(orr, orr, t)
                mul(t, ai, br)
                mul(oi, ar, bi)
                if neg:
                    link(v.scalar_tensor_tensor(oi, oi, -1.0, t, ALU.mult, ALU.subtract))
                else:
                    add(oi, oi, t)

            for k, w in ((1, 1), (2, 2), (4, 4)):
                b3 = lambda x: x[:, k:k + 1, :].broadcast_to([P, w, NPR])
                cmul(pr_[:, k + 1:k + 1 + w, :], pi_[:, k + 1:k + 1 + w, :], pr_[:, 1:1 + w, :], pi_[:, 1:1 + w, :],
                     b3(pr_), b3(pi_), TM[:, 0:w, 0:NPR])
            bsh = [P, NPR, GC]
            cb = lambda x: x.rearrange("p (n o) -> p n o", o=1).broadcast_to(bsh)
            pp = lambda nm: sp_(nm, NPR * GC).rearrange("p (n c) -> p n c", c=GC)
            cmul(BBR[:], BBI[:], cb(sv(12)), cb(sv(13)), pp("bre"), pp("bim"), BT[:])
            for s in range(S5L):
                k = S5L - 1 - s
                cmul(WR[:, :, s, :], WI[:, :, s, :], cb(pr_[:, k, :]), cb(pi_[:, k, :]), BBR[:], BBI[:], TM[:, :, 0:GC])
            dve.sem_inc(S("w_ready"), 1)
            for k in range(9):
                cmul(CPR[:, :, k, :], CPI[:, :, k, :], cb(pr_[:, k, :]), cb(pi_[:, k, :]), pp("cre"), pp("cim"),
                     TM[:, :, 0:GC], neg=True)
            dve.sem_inc(S("cp_ready"), 1)
            link(v.memset(TBR[:, :, 0:1], 1.0))
            link(v.memset(TBI[:, :, 0:1], 0.0))
            cur, nxt_ = (sv(9), sv(8)), (sv(16), sv(17))
            for _ in range(3):
                cmul(nxt_[0], nxt_[1], cur[0], cur[1], cur[0], cur[1], sv(15))
                cur, nxt_ = nxt_, ((sv(18), sv(19)) if nxt_[0] is not None and cur[0] is not None and _ % 2 == 0 else (sv(16), sv(17)))
            w = 1
            while w < NCH:
                sh = [P, NPR, w]
                b3 = lambda x: x.rearrange("p (n o) -> p n o", o=1).broadcast_to(sh)
                cmul(TBR[:, :, w:2 * w], TBI[:, :, w:2 * w], TBR[:, :, 0:w], TBI[:, :, 0:w], b3(cur[0]), b3(cur[1]), TM[:, :, 0:w])
                cmul(nxt_[0], nxt_[1], cur[0], cur[1], cur[0], cur[1], sv(15))
                cur, nxt_ = nxt_, cur
                w *= 2
            link(v.memset(D0[:], 0.0))
            link(v.tensor_tensor(D0[:, :, 1:NCH], D0[:, :, 1:NCH],
                                 sv(4).rearrange("p (n o) -> p n o", o=1).broadcast_to([P, NPR, NCH - 1]), ALU.add))
            dve.wait_ge(S("wt_full"), 8)
            v.memset(MM[:], 0.0).then_inc(S("mm_zero"), 1)
            dve.wait_ge(S("ks_evac"), 8)
            od = PCOLS["d"] - NSMALL
            dsh = [GC, NG, GC]
            ktmp = TM[0:GC, 0:4, :].rearrange("p a (b c) -> p (a b) c", c=GC)
            link(v.tensor_tensor(ktmp, ident[0:GC, 0:GC].rearrange("p (o c) -> p o c", o=1).broadcast_to(dsh),
                                 S5P[0:GC, od:od + NG].rearrange("p (g o) -> p g o", o=1).broadcast_to(dsh), ALU.mult))
            link(v.tensor_tensor(KS[:, :, 0:GC], KS[:, :, 0:GC], ktmp, ALU.add))
            dve.sem_inc(S("ks_d"), 1)
            dve.wait_ge(S("bu_full"), 2)
            dve.wait_ge(S("mm_in"), 8 * 16)
            f2 = lambda x: x[:].rearrange("p a b -> p (a b)")
            xr = PS[:, 4:8, :].rearrange("p a b -> p (a b)")
            xi = PS[:, 0:4, :].rearrange("p a b -> p (a b)")
            mul(f2(TM), xi, f2(TBI))
            mul(f2(GR), xr, f2(TBR))
            add(f2(GR), f2(GR), f2(TM))
            mul(f2(TM), xr, f2(TBI))
            mul(f2(GI), xi, f2(TBR))
            sub(f2(GI), f2(GI), f2(TM))
            for gg in (GR, GI):
                link(v.tensor_tensor_scan(f2(gg), f2(D0), f2(gg), 0.0, ALU.mult, ALU.add))
            cmul(f2(HR), f2(HI), f2(GR), f2(GI), f2(TBR), f2(TBI), f2(TM))
            dve.sem_inc(S("h_ready"), 1)
            for m in range(4):
                dve.wait_ge(S("yb_hi"), m + 1)
                v.tensor_tensor(GL[:, m, :], YB[:, m, :], GH[:, m, :].bitcast(F32), ALU.subtract).then_inc(S("yb_split"), 1)
            t0 = TILE0["glu"]
            for m in range(4):
                p = evac(t0 + m)
                if m >= 2:
                    dve.wait_ge(S("yb"), m - 1)
                v.tensor_copy(TT[1 + m % 2][:], p).then_inc(S("glu_evac"), 1)
                dve.wait_ge(S("glu_evac"), m + 1)
                dve.sem_inc(S("acc_free"), 1)
                dve.wait_ge(S("glu_sig"), m + 1)
                v.tensor_tensor(TT[1 + m % 2][:], TT[1 + m % 2][:], YB[:, m, :], ALU.mult).then_inc(S("glu_z"), 1)
                dve.wait_ge(S("z_hi"), m + 1)
                v.tensor_tensor(GL[:, 4 + m, :], TT[1 + m % 2][:], GH[:, 4 + m, :].bitcast(F32), ALU.subtract).then_inc(S("yb"), 1)

            dve.wait_ge(S("yb"), 4)
            for b in range(NBLK):
                n = (b + 1) * P
                sc, wk, bi, eq, pf = (x[:, 0:n] for x in (SC, WK, BI, EQ, PF))
                if n > TOPK:
                    for h in range(IH):
                        ib = (b - 2) * IH + h
                        dve.wait_ge(S("rl"), ib + 1)
                        iw = VV[:, b, AD + h:AD + h + 1]
                        if h == 0:
                            v.tensor_scalar(sc, RL[:, 0, 0:n], iw, None, ALU.mult).then_inc(S("sc"), 1)
                        else:
                            dve.wait_ge(S("sc"), ib)
                            v.scalar_tensor_tensor(sc, RL[:, h % 2, 0:n], iw, sc, ALU.mult, ALU.add).then_inc(S("sc"), 1)
                    dve.wait_ge(S("sc"), (b - 1) * IH)
                    link(v.memset(SC[0:CHUNK, n - CHUNK:n], NEG))
                    link(v.max(sm2[:], sc))
                    for r in range(TOPK // 8 - 1):
                        link(v.match_replace(wk, sm2[:], sc if r == 0 else wk, 2 * NEG))
                        link(v.max(sm2[:], wk))
                    thr = sm2[:, 7:8]
                    link(v.tensor_scalar(eq, sc, thr, 0.0, ALU.is_gt, ALU.add, accum_out=sm1[:, 6:7]))
                    link(v.tensor_scalar(sm1[:, 6:7], sm1[:, 6:7], -1.0, float(TOPK), ALU.mult, ALU.add))
                    link(v.tensor_scalar(eq, sc, thr, None, ALU.is_equal))
                    link(v.tensor_tensor_scan(pf, eq, eq, 0.0, ALU.add, ALU.max))
                    link(v.scalar_tensor_tensor(pf, pf, sm1[:, 6:7], eq, ALU.is_le, ALU.mult))
                    link(v.scalar_tensor_tensor(bi, sc, thr, pf, ALU.is_gt, ALU.add))
                    link(v.tensor_scalar(bi, bi, -1.0, -NEG, ALU.add, ALU.mult))
                else:
                    link(v.memset(bi, 0.0))
                    link(v.memset(BI[0:CHUNK, n - CHUNK:n], NEG))

                def head_max(h):
                    i = b * AH + h
                    j = i % 2
                    dve.wait_ge(S("s_full"), i + 1)
                    if i >= 2:
                        dve.wait_ge(S("p_exp"), i - 1)
                    v.tensor_tensor_reduce(MS[j][:, 0:n], bank2(4 + 2 * (h % 2))[:, 0:n], bi, 1.0, 4 * NEG, ALU.add,
                                           ALU.max, sm1[:, j:j + 1]).then_inc(S("ms_full"), 1)
                    dve.wait_ge(S("ms_full"), i + 1)
                    v.scalar_tensor_tensor(sm1[:, 2 + j:3 + j], sm1[:, j:j + 1], -1.0, fq[:, b * 8 + h:b * 8 + h + 1],
                                           ALU.mult, ALU.mult).then_inc(S("nmax"), 1)

                def head_norm(h):
                    i = b * AH + h
                    j = i % 2
                    dve.wait_ge(S("p_exp"), i + 1)
                    link(v.reciprocal(sm1[:, 4 + j:5 + j], sm1[:, 4 + j:5 + j]))
                    v.tensor_scalar(PP[j][:, 0:n], PP[j][:, 0:n], sm1[:, 4 + j:5 + j], None, ALU.mult).then_inc(S("p_ready"), 1)

                head_max(0)
                for h in range(AH):
                    if h + 1 < AH:
                        head_max(h + 1)
                    head_norm(h)
                dve.wait_ge(S("ya_hi"), b + 1)
                v.tensor_tensor(GL[:, 0:4, b * P:(b + 1) * P], PS[:, 2 + b % 2, :].rearrange("p (a b) -> p a b", a=4),
                                GH[:, 0:4, b * P:(b + 1) * P].bitcast(F32), ALU.subtract).then_inc(S("ya"), 1)
            dve.wait_ge(S("ya"), NBLK)
            dve.sem_inc(S("x_free"), 1)

            def residual(t0, tag, add_, split=True):
                dve.wait_ge(S("acc_free"), t0)
                for m in range(KT):
                    p = evac(t0 + m)
                    v.tensor_tensor(X[:, m, :], X[:, m, :], p, ALU.add).then_inc(S("x"), 1)
                    dve.wait_ge(S("x"), norm_base("x", tag) + m + 1)
                    dve.sem_inc(S("acc_free"), 1)
                    if split and m >= 1:
                        gxlo(tag, m - 1)
                if split:
                    gxlo(tag, KT - 1)
                    sq_done(tag)

            dve.wait_ge(S("x_back"), 16)
            t0 = TILE0["out"]
            for m in range(KT):
                p = evac(t0 + m)
                link(v.tensor_tensor(X[:, m, :], X[:, m, :], p, ALU.add))
                dve.sem_inc(S("acc_free"), 1)
            dve.sem_inc(S("x"), KT)
            for k in range(KT):
                gxlo("x0", k)
            sq_done("x0")

            def cross(l):
                dve.sem_inc(S("me_free"), 1)
                dve.wait_ge(S("me_in"), 16 * l + 16)
                for k in range(KT):
                    if k == 0:
                        link(v.tensor_tensor(MR[:, 0, :], ME[:, k, :], ME[:, k, :], ALU.mult))
                    else:
                        link(v.tensor_tensor(MR[:, 1, :], ME[:, k, :], ME[:, k, :], ALU.mult))
                        link(v.tensor_tensor(MR[:, 0, :], MR[:, 0, :], MR[:, 1, :], ALU.add))
                dve.sem_inc(S("me_sq"), 1)
                dve.wait_ge(S("me_rms"), 1 * l + 1)
                link(v.reciprocal(MR[:, 1, :], MR[:, 1, :]))
                for k in range(KT):
                    v.scalar_tensor_tensor(ME[:, k, :], ME[:, k, :], par(f"mem{l}", k), MR[:, 1, :], ALU.mult,
                                           ALU.mult).then_inc(S("me_n"), 1)
                for k in range(KT):
                    dve.wait_ge(S("mh"), 8 * l + k + 1)
                    v.tensor_tensor(ML[:, k, :], ME[:, k, :], MH[:, k, :].bitcast(F32), ALU.subtract).then_inc(S("me_split"), 1)
                t0 = TILE0[f"xk{l}"]
                for m in range(4):
                    p = evac(t0 + m)
                    link(v.tensor_copy(XKt[:, m, :], p[:, 0:M]))
                    dve.sem_inc(S("acc_free"), 1)
                dve.sem_inc(S("xk_raw"), 1)
                p = evac(TILE0[f"xv{l}"])
                link(v.tensor_copy(XV[:].rearrange("p a b -> p (a b)"), p))
                dve.sem_inc(S("acc_free"), 1)
                dve.wait_ge(S("xk_rms"), 1 * l + 1)
                link(v.reciprocal(TT[4][:], TT[3][:]))
                link(v.tensor_tensor(sm1[:, 0:1], par(f"xq{l}"), par(f"xk{l}"), ALU.mult))
                link(v.scalar_tensor_tensor(XKt[:].rearrange("p a b -> p (a b)"), XKt[:].rearrange("p a b -> p (a b)"),
                                            sm1[:, 0:1], TT[4][:], ALU.mult, ALU.mult))
                dve.sem_inc(S("xk_ready"), 1)
                t0 = TILE0[f"xq{l}"]
                for m in range(4):
                    p = evac(t0 + m)
                    v.tensor_copy(XQ[:, m, :], p).then_inc(S("xq_copy"), 1)
                    dve.wait_ge(S("xq_copy"), 4 * l + m + 1)
                    dve.sem_inc(S("acc_free"), 1)
                norm(f"x{l}", both=False)
                link(v.tensor_tensor(rTa[:], rT[:], rT[:], ALU.mult))
                dve.wait_ge(S("xq_ms"), 4 * l + 4)
                f3 = lambda x: x[:, 0:32].rearrange("p (b h) -> p b h", h=XH)
                bc = lambda x: x[:].rearrange("p (b o) -> p b o", o=1).broadcast_to([P, NBLK, XH])
                v.tensor_tensor(f3(fq), PS[:, 7, 0:32].rearrange("p (b h) -> p b h", h=XH), bc(rTa), ALU.mult).then_inc(S("xq_var"), 1)
                dve.wait_ge(S("xq_rms"), 1 * l + 1)
                link(v.reciprocal(fqa[:, 0:32], fqa[:, 0:32]))
                link(v.scalar_tensor_tensor(f3(fq), f3(fqa), P ** -0.5, bc(rT), ALU.mult, ALU.mult))
                dve.sem_inc(S("xfq"), 1)
                for b in range(NBLK):
                    dve.wait_ge(S("xs_full"), 8 * l + b + 1)
                    s3 = bank2(4).rearrange("p (h m) -> p h m", h=XH)
                    link(v.tensor_reduce(sm1[:, 4:8], s3, AXX, ALU.max))
                    v.scalar_tensor_tensor(sm1[:, 0:4], sm1[:, 4:8], -1.0, fq[:, 4 * b:4 * b + 4], ALU.mult,
                                           ALU.mult).then_inc(S("xnmax"), 1)
                    dve.wait_ge(S("xp_exp"), 8 * l + b + 1)
                    dve.sem_inc(S("xs_read"), 1)
                    link(v.reciprocal(sm2[:, 4:8], sm2[:, 0:4]))
                    v.tensor_tensor(XP[b % 2][:], XP[b % 2][:],
                                    sm2[:, 4:8].rearrange("p (h o) -> p h o", o=1).broadcast_to([P, XH, M]),
                                    ALU.mult).then_inc(S("xp"), 1)
                    dve.wait_ge(S("oh"), 8 * l + b + 1)
                    v.tensor_tensor(OL[:, :, b * P:(b + 1) * P], PS[:, b % 2, :].rearrange("p (a b) -> p a b", a=4),
                                    OH[:, :, b * P:(b + 1) * P].bitcast(F32), ALU.subtract).then_inc(S("xo_evac"), 1)
                residual(TILE0[f"xo{l}"], f"ffn{l}", None)

            def grouped(tag, l, nup, ngrp, nxt):
                norm(GROUPED_NORM[tag])
                dve.wait_ge(S("R"), norm_base("R", GROUPED_NORM[tag]) + 1)
                link(v.memset(T0[:, 0:2], 0.0))
                if tag == "odd":
                    link(v.tensor_tensor(TT[4][:], R[:], R[:], ALU.mult))
                t0 = TILE0[tag]
                tper = nup + 8

                def taps(f):
                    if tag == "odd":
                        return par("ocw", f), par("ocw", 8 + f)
                    c0 = PCOLS[f"fcw{l}"]
                    if isinstance(f, int):
                        return PAR[:, c0 + f:c0 + f + 1], PAR[:, c0 + FT + f:c0 + FT + f + 1]
                    return PAR[:, bass.ds(f + c0, 1)], PAR[:, bass.ds(f + (c0 + FT), 1)]

                def tile(f, cnt, j, t, it=0, tit=0, used=None):
                    c = it + cnt
                    w0, w1 = taps(f)
                    p = evac(t, tit)
                    if tag == "odd":
                        v.tensor_tensor(TT[3][:], p, TT[4][:], ALU.mult).then_inc(S("acc_free"), 1)
                        p = evac(t + 1, tit)
                        dve.wait_ge(S("acc_free"), tit + (t + 1))
                        v.tensor_tensor(T0[:, 2:T + 2], p, TT[3][:], ALU.mult).then_inc(S("sig"), 1)
                    else:
                        v.tensor_tensor(T0[:, 2:T + 2], p, R[:], ALU.mult).then_inc(S("sig"), 1)
                    dve.wait_ge(S("sig"), grouped_base("sig", tag) + c + 1)
                    dve.sem_inc(S("acc_free"), 1)
                    dve.wait_ge(S("tap"), grouped_base("tap", tag) + c + 1)
                    v.scalar_tensor_tensor(TT[1][:], T0[:, 1:T + 1], w1, TT[1][:], ALU.mult, ALU.add).then_inc(S("c1"), 1)
                    dve.wait_ge(S("c1"), grouped_base("c1", tag) + c + 1)
                    v.scalar_tensor_tensor(TT[1][:], T0[:, 0:T], w0, TT[1][:], ALU.mult, ALU.add).then_inc(S("conv"), 1)
                    p = evac(t + nup // GRP - 1, tit)
                    v.tensor_tensor(TT[2][:], p, R[:], ALU.mult).then_inc(S("acc_free"), 1)
                    last = "act" if tag != "odd" else "conv"
                    dve.wait_ge(S(last), grouped_base(last, tag) + c + 1)
                    dve.wait_ge(S("acc_free"), tit + (t + nup // GRP))
                    if used is not None:
                        dve.wait_ge(S("used"), grouped_base("used", tag) + used)
                    v.tensor_tensor(TT[2][:], TT[2][:], TT[1][:], ALU.mult).then_inc(S("h"), 1)
                    dve.wait_ge(S("hh"), grouped_base("hh", tag) + c + 1)
                    v.tensor_tensor(HL[:, j, :], TT[2][:], HH[:, j, :].bitcast(F32), ALU.subtract).then_inc(S("hid"), 1)

                def down(t, tit=0):
                    for m in range(KT):
                        p = evac(t + m, tit)
                        v.tensor_tensor(X[:, m, :], X[:, m, :], p, ALU.add).then_inc(S("acc_free"), 1)

                step = nup // GRP
                for j in range(GRP):
                    tile(j, j, j, t0 + step * j)
                pairs = (ngrp - 1) // 2
                t1 = t0 + nup
                if pairs > 1:
                    with dve.Fori(0, pairs) as i:
                        it, tit = i * (2 * GRP), i * (2 * tper)
                        for q in range(2):
                            for j in range(GRP):
                                c = GRP * (q + 1) + j
                                tile(it + c, c, c % (2 * GRP), t1 + q * tper + step * j, it, tit,
                                     used=i * 2 + q)
                            down(t1 + q * tper + nup, tit)
                    g = 2 * pairs
                    t1 += g * tper
                else:
                    g = 0
                while g < ngrp - 1:
                    for j in range(GRP):
                        c = GRP * (g + 1) + j
                        tile(c, c, c % (2 * GRP), t1 + step * j, used=g if g >= 1 else None)
                    down(t1 + nup)
                    t1 += tper
                    g += 1
                if nxt:
                    residual(t1, nxt, None)
                else:
                    residual(t1, "end", None, split=False)

            cross(0)
            grouped("mlp0", 0, 4, NGRP, "mix1")
            grouped("odd", 1, 6, OGRP, "x1")
            cross(1)
            grouped("mlp1", 1, 4, NGRP, None)


def kernel(**inputs):
    import numpy as np
    import concourse.bacc as _bacc
    from concourse import mybir as _mybir
    from concourse.bass_utils import run_bass_kernel_spmd as _run

    I = {k: np.ascontiguousarray(a) for k, a in inputs.items()}
    panels = []

    def tiles(w):
        k, m = w.shape
        return w.reshape(k // P, P, m // P, P).transpose(2, 1, 0, 3)

    def full(w):
        panels.extend(tiles(w))

    def packed(w, per):
        t = tiles(w)
        for i in range(0, t.shape[0], per):
            panels.append(t[i:i + per].transpose(1, 0, 2, 3).reshape(P, 8, P))

    w = I["even_w_in"][0]
    q, kk, v, iq, ik, iw, u = (w[:, a:b] for a, b in zip(
        (0, 512, 576, 640, 896, 960, 964), (512, 576, 640, 896, 960, 964, 1476)))
    full(np.concatenate([q, kk, kk, iq, ik, ik, u], axis=1))
    wv = np.concatenate([v, iw], axis=1).reshape(KT, P, VW).transpose(1, 0, 2)
    packed(I["s5_w_glu"][0], 2)
    full(I["even_w_out"][0])

    def cross(l):
        wk, wvv = I["x_w_kv"][l][:, :512], I["x_w_kv"][l][:, 512:]
        full(wk)
        for m in range(4):
            panels.append(wvv[2 * m * P:2 * (m + 1) * P].reshape(2, P, 4, P).transpose(1, 0, 2, 3).reshape(P, 8, P))
        full(I["x_w_q"][l])
        packed(I["x_w_o"][l], 2)

    def grouped(ups, wdown, ngrp):
        def up(g):
            for f in range(GRP * g, GRP * g + GRP):
                panels.extend(ups(f))

        def down(g):
            packed(wdown[GRP * g * P:GRP * (g + 1) * P], 4)
        up(0)
        for g in range(1, ngrp):
            up(g)
            down(g - 1)
        down(ngrp - 1)

    def mlp(l):
        g, u_ = tiles(I["f_w_up"][l][:, :FF]), tiles(I["f_w_up"][l][:, FF:])
        grouped(lambda f: [g[f], u_[f]], I["f_w_down"][l], NGRP)

    cross(0)
    mlp(0)
    gb, gc, z = (tiles(I["odd_w_in"][0][:, i * D:(i + 1) * D]) for i in range(3))
    grouped(lambda f: [gc[f], z[f], gb[f]], I["odd_w_out"][0], OGRP)
    cross(1)
    mlp(1)
    assert len(panels) == NPANEL, (len(panels), NPANEL)

    par = np.zeros((P, NPAR), np.float32)

    def put(name, a):
        par[:a.shape[0], PCOLS[name]:PCOLS[name] + a.shape[1]] = a

    col = lambda a: a.reshape(-1, P).T
    for l in range(2):
        for nm, src in (("mix", "norm_mix"), ("x", "norm_x"), ("mem", "norm_mem"), ("ffn", "norm_ffn")):
            put(f"{nm}{l}", col(I[src][l]))
        put(f"xq{l}", col(I["x_q_norm"][l]))
        put(f"xk{l}", col(I["x_k_norm"][l]))
        put(f"fcw{l}", col(I["f_conv_w"][l]))
        put(f"fcb{l}", col(I["f_conv_b"][l]))
    put("aq", np.tile(I["a_q_norm"][0], 2)[:, None])
    put("ak", np.tile(I["a_k_norm"][0], 2)[:, None])
    put("bglu", col(I["s5_b_glu"][0]))
    put("ocw", col(I["odd_conv_w"][0]))
    put("ocb", col(I["odd_conv_b"][0]))
    pairs = lambda a: a.reshape(NPR, 2, NS, -1).transpose(1, 2, 0, 3).reshape(P, -1)
    put("lre", pairs(I["s5_lam_re"][0]))
    put("lim", pairs(I["s5_lam_im"][0]))
    put("lstep", np.repeat(I["s5_log_step"][0].reshape(NPR, 2).T, NS, axis=0))
    put("bre", pairs(I["s5_b_re"][0]))
    put("bim", pairs(I["s5_b_im"][0]))
    put("cre", pairs(I["s5_c_re"][0].transpose(0, 2, 1)))
    put("cim", pairs(I["s5_c_im"][0].transpose(0, 2, 1)))
    put("d", I["s5_d"][0].reshape(NG, GC).T)

    arrays = {
        "xT": np.ascontiguousarray(I["x"][0].T),
        "memT": np.ascontiguousarray(I["mem"][0].T),
        "panels": np.ascontiguousarray(np.stack(panels)),
        "wv": np.ascontiguousarray(wv),
        "par": par,
    }
    nc = _bacc.Bacc("TRN2", target_bir_lowering=False, num_devices=1)
    aps = {n: nc.dram_tensor(n, a.shape, _mybir.dt.from_np(a.dtype), kind="ExternalInput").ap()
           for n, a in arrays.items()}
    aps["outT"] = nc.dram_tensor("outT", (D, T), _mybir.dt.float32, kind="ExternalOutput").ap()
    build(nc, aps)
    r = _run(nc, [arrays], core_ids=[0])
    return np.ascontiguousarray(r.results[0]["outT"].T)[None]
```
